# Optimizing a Trainium2 kernel written in Bass

```python
import jax, jax.numpy as jnp
from jax import lax
import numpy as np

D_MODEL = 1024
BATCH = 1
SEQ = 256
DEPTH = 1
DEC_BATCH = 8
DEC_SEQ = 8
PAST_LEN = 2048
PAGE_SIZE = 128

MIX_WIDTH = D_MODEL
POOL_WIDTH = MIX_WIDTH // 2
GMLP_WIDTH = MIX_WIDTH - POOL_WIDTH
POOL_WINDOWS = (2, 4, 8, 16)
N_POOL_GROUPS = len(POOL_WINDOWS)
POOL_GROUP = POOL_WIDTH // N_POOL_GROUPS
POOL_HIST = max(POOL_WINDOWS) - 1
CHUNK = 128
N_GMLP_HEADS = 4
GMLP_HEAD = GMLP_WIDTH // N_GMLP_HEADS
IN_WIDTH = POOL_WIDTH + 2 * GMLP_WIDTH
N_EXPERT_GROUPS = 4
EXPERTS_PER_GROUP = 8
N_EXPERTS = N_EXPERT_GROUPS * EXPERTS_PER_GROUP
TOP_K_INNER = 2
D_EXPERT = D_MODEL // 2
PLE_DIM = 256
EPS = 1e-6

kernel_name = 'hybrid_pool_gmlp_hmoe_decode_step'

def rmsnorm(x, g):
    xf = x.astype(jnp.float32)
    y = xf * lax.rsqrt(jnp.mean(xf * xf, axis=-1, keepdims=True) + EPS) * g.astype(jnp.float32)
    return y.astype(x.dtype)

def layernorm(x, g, b):
    xf = x.astype(jnp.float32)
    mu = jnp.mean(xf, axis=-1, keepdims=True)
    xc = xf - mu
    y = xc * lax.rsqrt(jnp.mean(xc * xc, axis=-1, keepdims=True) + EPS)
    return (y * g.astype(jnp.float32) + b.astype(jnp.float32)).astype(x.dtype)

def pool_mix(a, hist, pos0, w_pool, pool_scale):
    B, L, _ = a.shape
    ext = jnp.concatenate([hist.astype(jnp.float32), a.astype(jnp.float32)], axis=1)
    csum = jnp.concatenate([jnp.zeros((B, 1, POOL_WIDTH), jnp.float32),
                            jnp.cumsum(ext, axis=1)], axis=1)
    pos = pos0 + jnp.arange(L)
    cur = ext[:, POOL_HIST:]
    outs = []
    for gi, w in enumerate(POOL_WINDOWS):
        sl = slice(gi * POOL_GROUP, (gi + 1) * POOL_GROUP)
        win_sum = (csum[:, POOL_HIST + 1:POOL_HIST + 1 + L, sl]
                   - csum[:, POOL_HIST + 1 - w:POOL_HIST + 1 - w + L, sl])
        cnt = jnp.minimum(w, pos + 1).astype(jnp.float32)
        outs.append(win_sum / cnt[None, :, None] - cur[..., sl])
    pooled = jnp.stack(outs, axis=2)
    y = jnp.einsum('blgc,gcd->blgd', pooled, w_pool.astype(jnp.float32)).reshape(B, L, POOL_WIDTH)
    y = y * pool_scale.astype(jnp.float32)
    new_hist = ext[:, -POOL_HIST:]
    return y.astype(a.dtype), new_hist.astype(a.dtype)

def spatial_gate(u, v, w_spatial, b_spatial):
    B, L, _ = u.shape
    Lc = -(-L // CHUNK) * CHUNK
    nc = Lc // CHUNK
    vp = jnp.pad(v, ((0, 0), (0, Lc - L), (0, 0))).reshape(B, nc, CHUNK, N_GMLP_HEADS, GMLP_HEAD)
    mask = jnp.tril(jnp.ones((CHUNK, CHUNK), dtype=bool))
    w = jnp.where(mask[None], w_spatial, jnp.zeros_like(w_spatial))
    mixed = jnp.einsum('hts,bcshd->bcthd', w, vp) + jnp.transpose(b_spatial)[None, None, :, :, None]
    mixed = mixed.reshape(B, Lc, GMLP_WIDTH)[:, :L]
    return u * mixed

def hier_moe(x, w_rg, b_rg, w_re, b_re, w_eg, w_eu, w_ed):
    N = x.shape[0]
    g_logits = (x @ w_rg + b_rg).astype(jnp.float32)
    g_prob = jax.nn.softmax(g_logits, axis=-1)
    _, g_idx = lax.top_k(g_logits, 1)
    e_logits = (x @ w_re + b_re).astype(jnp.float32).reshape(N, N_EXPERT_GROUPS, EXPERTS_PER_GROUP)
    e_sel = jnp.take_along_axis(e_logits, g_idx[:, :, None], axis=1)[:, 0]
    e_val, e_idx = lax.top_k(e_sel, TOP_K_INNER)
    e_w = jax.nn.softmax(e_val, axis=-1) * jnp.take_along_axis(g_prob, g_idx, axis=1)
    flat = g_idx * EXPERTS_PER_GROUP + e_idx
    combine = jnp.sum(jax.nn.one_hot(flat, N_EXPERTS, dtype=jnp.float32) * e_w[..., None], axis=1)
    out = jnp.zeros((N, x.shape[1]), jnp.float32)
    for e in range(N_EXPERTS):
        h = jax.nn.silu(x @ w_eg[e]) * (x @ w_eu[e])
        out = out + combine[:, e:e + 1] * (h @ w_ed[e]).astype(jnp.float32)
    return out.astype(x.dtype)

def decoder_layer(x, p, hist, pos0, g_mix, w_in, w_pool, pool_scale, g_v, b_v, w_spatial,
                  b_spatial, w_out, g_ffn, w_rg, b_rg, w_re, b_re, w_eg, w_eu, w_ed,
                  w_ple, g_ple, w_ple_gate):
    B, L, D = x.shape
    xn = rmsnorm(x, g_mix)
    z = xn @ w_in
    a = z[..., :POOL_WIDTH]
    uv = jax.nn.gelu(z[..., POOL_WIDTH:])
    u = uv[..., :GMLP_WIDTH]
    v = layernorm(uv[..., GMLP_WIDTH:], g_v, b_v)
    pool_out, new_hist = pool_mix(a, hist, pos0, w_pool, pool_scale)
    gmlp_out = spatial_gate(u, v, w_spatial, b_spatial)
    h = x + jnp.concatenate([pool_out, gmlp_out.astype(pool_out.dtype)], axis=-1) @ w_out
    hn = rmsnorm(h, g_ffn).reshape(B * L, D)
    h = h + hier_moe(hn, w_rg, b_rg, w_re, b_re, w_eg, w_eu, w_ed).reshape(B, L, D)
    gate = jax.nn.sigmoid((rmsnorm(h, g_ple) @ w_ple_gate).astype(jnp.float32))
    h = h + ((p @ w_ple).astype(jnp.float32) * gate).astype(h.dtype)
    v_open = v[:, ((L - 1) // CHUNK) * CHUNK:]
    return h, new_hist, v_open

def setup_inputs(seed: int = 0) -> dict:
    key = jax.random.key(seed)
    ks = jax.random.split(key, 32)
    f = jnp.float32
    nrm = lambda k, shape, s: jax.random.normal(k, shape, f) * s
    gain = lambda k, shape: 1.0 + 0.05 * jax.random.normal(k, shape, f)
    return {
        'x_prompt': nrm(ks[0], (BATCH, SEQ, D_MODEL), 1.0),
        'x_sample': nrm(ks[1], (DEC_BATCH, DEC_SEQ, D_MODEL), 1.0),
        'state_pool': nrm(ks[2], (DEPTH, DEC_BATCH, POOL_HIST, POOL_WIDTH), 0.5),
        'p_prompt': nrm(ks[3], (DEPTH, BATCH, SEQ, PLE_DIM), 1.0),
        'p_sample': nrm(ks[4], (DEPTH, DEC_BATCH, DEC_SEQ, PLE_DIM), 1.0),
        'g_mix': gain(ks[5], (DEPTH, D_MODEL)),
        'w_in': nrm(ks[6], (DEPTH, D_MODEL, IN_WIDTH), D_MODEL ** -0.5),
        'w_pool': nrm(ks[7], (DEPTH, N_POOL_GROUPS, POOL_GROUP, POOL_GROUP), POOL_GROUP ** -0.5),
        'pool_scale': gain(ks[8], (DEPTH, POOL_WIDTH)),
        'g_v': gain(ks[9], (DEPTH, GMLP_WIDTH)),
        'b_v': nrm(ks[10], (DEPTH, GMLP_WIDTH), 0.02),
        'w_spatial': nrm(ks[11], (DEPTH, N_GMLP_HEADS, CHUNK, CHUNK), CHUNK ** -0.5),
        'b_spatial': gain(ks[12], (DEPTH, N_GMLP_HEADS, CHUNK)),
        'w_out': nrm(ks[13], (DEPTH, MIX_WIDTH, D_MODEL), MIX_WIDTH ** -0.5),
        'g_ffn': gain(ks[14], (DEPTH, D_MODEL)),
        'w_rg': nrm(ks[15], (DEPTH, D_MODEL, N_EXPERT_GROUPS), D_MODEL ** -0.5),
        'b_rg': nrm(ks[16], (DEPTH, N_EXPERT_GROUPS), 0.01),
        'w_re': nrm(ks[17], (DEPTH, D_MODEL, N_EXPERTS), D_MODEL ** -0.5),
        'b_re': nrm(ks[18], (DEPTH, N_EXPERTS), 0.01),
        'w_eg': nrm(ks[19], (DEPTH, N_EXPERTS, D_MODEL, D_EXPERT), D_MODEL ** -0.5),
        'w_eu': nrm(ks[20], (DEPTH, N_EXPERTS, D_MODEL, D_EXPERT), D_MODEL ** -0.5),
        'w_ed': nrm(ks[21], (DEPTH, N_EXPERTS, D_EXPERT, D_MODEL), D_EXPERT ** -0.5),
        'w_ple': nrm(ks[22], (DEPTH, PLE_DIM, D_MODEL), PLE_DIM ** -0.5),
        'g_ple': gain(ks[23], (DEPTH, D_MODEL)),
        'w_ple_gate': nrm(ks[24], (DEPTH, D_MODEL, D_MODEL), D_MODEL ** -0.5),
        'g_final': gain(ks[25], (D_MODEL,)),
    }

def reference(x_prompt, x_sample, state_pool, p_prompt, p_sample, g_mix, w_in, w_pool,
              pool_scale, g_v, b_v, w_spatial, b_spatial, w_out, g_ffn, w_rg, b_rg, w_re,
              b_re, w_eg, w_eu, w_ed, w_ple, g_ple, w_ple_gate, g_final):
    hp = x_prompt
    hs = x_sample
    zero_hist = jnp.zeros((x_prompt.shape[0], POOL_HIST, POOL_WIDTH), x_prompt.dtype)
    pool_p, pool_s, vchunk_s = [], [], []
    for i in range(DEPTH):
        lw = (g_mix[i], w_in[i], w_pool[i], pool_scale[i], g_v[i], b_v[i], w_spatial[i],
              b_spatial[i], w_out[i], g_ffn[i], w_rg[i], b_rg[i], w_re[i], b_re[i],
              w_eg[i], w_eu[i], w_ed[i], w_ple[i], g_ple[i], w_ple_gate[i])
        hp, hist_p, _ = decoder_layer(hp, p_prompt[i], zero_hist, 0, *lw)
        hs, hist_s, v_s = decoder_layer(hs, p_sample[i], state_pool[i], PAST_LEN, *lw)
        pool_p.append(hist_p)
        pool_s.append(hist_s)
        vchunk_s.append(v_s)
    y_prompt = rmsnorm(hp, g_final)
    y_sample = rmsnorm(hs, g_final)
    new_pool_prompt = jnp.stack(pool_p, axis=0)
    new_pool_sample = jnp.stack(pool_s, axis=0)
    new_vchunk_sample = jnp.stack(vchunk_s, axis=0)
    return (y_prompt, y_sample, new_pool_prompt, new_pool_sample, new_vchunk_sample)


_drawn_inputs = setup_inputs


def setup_inputs(seed=0):
    import zlib

    import numpy as np

    out = dict(_drawn_inputs(seed))
    spreads = {}
    factors = {'b_v': 2.726, 'b_rg': 4.766, 'b_re': 5.126, 'g_ple': 7.73}
    for name, (base, spread) in spreads.items():
        noise = np.random.default_rng([zlib.crc32(name.encode()), seed]).standard_normal(out[name].shape)
        drawn = base * np.exp(spread * noise) if base else spread * noise
        out[name] = __import__('jax').numpy.asarray(drawn.astype(out[name].dtype))
    for name, factor in factors.items():
        out[name] = (out[name] * factor).astype(out[name].dtype)
    return out
```

```python
from contextlib import ExitStack

import numpy as np

import concourse.bass as bass
from concourse import mybir
from concourse.alu_op_type import AluOpType as ALU

ACT = mybir.ActivationFunctionType
AX = mybir.AxisListType
F32 = mybir.dt.float32
F32R = mybir.dt.float32r
BF16 = mybir.dt.bfloat16
I32 = mybir.dt.int32
U32 = mybir.dt.uint32

P = 128
D = 1024
KC = D // P
SEQ, DEC_B, DEC_L = 256, 8, 8
NS = DEC_B * DEC_L
NT = SEQ + NS
TILES = 3
ROWS = [P, P, NS]
W = 512
NG = 4
HIST = 15
EXT_S = SEQ + HIST
EXT_B = HIST + DEC_L
EXT = EXT_S + DEC_B * EXT_B
NE = 32
PLE = 256
EPS = 1e-6
BIG = 3.0e38

SLOTS = 48
PASSES = -(-NT // SLOTS)
HALF = 64
PAIRS = NE // 2
RING = 6
BLOCK = 512
MBLOCKS = 8
UBLOCKS = 4
SBLOCKS = 3
SPLIT = SBLOCKS * BLOCK
UNITS = 12
ROUNDS = PAIRS + 1
HI_RING, LO_RING = 4, 3
NOWHERE = 4096.0
EMPTY = 1024


def need(eng, sem, value):
    if not (isinstance(value, int) and value <= 0):
        eng.wait_ge(sem, value)


def chain(eng, sem):
    count = [0]

    def link(ins):
        count[0] += 1
        ins.then_inc(sem, 1)
        eng.wait_ge(sem, count[0])
    return link


def build(nc, x_prompt, x_sample, state_pool, p_prompt, p_sample, g_mix, w_in, w_pool, pool_scale,
          g_v, b_v, w_spatial, b_spatial, w_out, g_ffn, w_rg, b_rg, w_re, b_re, w_eg, w_eu, w_ed,
          w_ple, g_ple, w_ple_gate, g_final,
          y_prompt, y_sample, new_pool_prompt, new_pool_sample, new_vchunk):
    ctx = ExitStack()
    with ctx:
        ctx.enter_context(nc.allow_non_contiguous_dma(reason="small transposed weights"))

        def sem(name):
            return ctx.enter_context(nc.semaphore(name))

        hn_rows = nc.dram_tensor("hn_rows", (NT, D), F32, kind="Internal").ap()
        moe_rows = nc.dram_tensor("moe_rows", (2 * NT, D), F32, kind="Internal").ap()

        def by_tile(prompt, sample):
            return [prompt[0:P, :], prompt[P:SEQ, :], sample]

        x_rows = by_tile(x_prompt[0], x_sample.rearrange("b l d -> (b l) d"))
        p_rows = by_tile(p_prompt[0, 0], p_sample[0].rearrange("b l d -> (b l) d"))
        y_rows = by_tile(y_prompt[0], y_sample.rearrange("b l d -> (b l) d"))
        w_in_v = w_in[0].rearrange("(p k) n -> p k n", k=KC)
        w_out_v = w_out[0].rearrange("(k p) n -> p k n", p=P)
        w_gate_v = w_ple_gate[0].rearrange("(p k) n -> p (k n)", k=KC)

        def sb(name, shape, dt=F32, stack=ctx):
            return stack.enter_context(nc.sbuf_tensor(name, shape, dt))

        ring = sb("ring", [P, RING, MBLOCKS * BLOCK])
        h = sb("h", [P, TILES, D])
        ple = sb("ple", [P, TILES, D])
        w_ple_sb = sb("w_ple_sb", [P, 2, D])
        xg = sb("xg", [2 * SLOTS, D])
        ident = sb("ident", [P, P])
        fold = sb("fold", [P, SLOTS])
        stat = sb("stat", [P, 16, TILES])
        cw = sb("cw", [P, 2, TILES])
        place = sb("place", [P, TILES, NE])
        tok = sb("tok", [P, TILES, 3], BF16)
        e_row = sb("e_row", [P, NE])
        row_in = sb("row_in", [SLOTS, NE + 2], I32)
        row_out = sb("row_out", [SLOTS, NE + 2], I32)
        cur = sb("cur", [SLOTS, 3], I32)
        most = sb("most", [P, 1], I32)
        spare = sb("spare", [1, 2])

        with ExitStack() as mixer:
            def sa(name, shape, dt=F32):
                return sb(name, shape, dt, mixer)

            perm = sa("perm", [P, TILES, KC, P])
            nT = sa("nT", [P, KC, TILES * P])
            mixT = sa("mixT", [P, KC, NT])
            vt = sa("vt", [P, TILES, W])
            g_row = sa("g_row", [P, D])
            wsT = sa("wsT", [P, NG, P])
            rt = sa("rt", [P, KC, NG + NE])
            cols = sa("cols", [P, 4 + 4 * 16 + 16 + 6 * TILES + 2 * TILES])
            rows = sa("rows", [1, P + NG * P + NG * NS])
            sa("spacer", [P, 36])
            ext = sa("ext", [P, NG, EXT])
            win = sa("win", [P, 2, NG, EXT])
            low_ones = sa("low_ones", [P, 2, P], BF16)
            b_col = sa("b_col", [NG + NE, 1])
        with ExitStack() as experts:
            hi = sb("hi", [P, HI_RING, SPLIT], F32R, experts)
            lo = sb("lo", [P, LO_RING, SPLIT], F32R, experts)
            xr = sb("xr", [P, KC, 2, 2, HALF], F32R, experts)
            xz = sb("xz", [P, 2, 2, P], F32, experts)
            h32 = sb("h32", [P, 4, P], F32, experts)
            hr = sb("hr", [P, 4, 2, HALF], F32R, experts)
            gu = sb("gu", [P, 2, 4, P], F32, experts)
            sg = sb("sg", [P, 4, SLOTS], F32, experts)
            yc = sb("yc", [SLOTS, D], F32, experts)
            yo = sb("yo", [SLOTS, D], F32, experts)

        p_tok = mixT[:, 0:3, 0:PLE]
        pT = ple[:, 2, D - 2 * TILES * P:D].rearrange("p (k t) -> p k t", k=2)
        small_w = ring[:, 5, 0:2 * D]
        gv_row, bv_row = ring[:, 5, 2 * D:2 * D + W], ring[:, 5, 2 * D + W:3 * D]
        wsp = small_w[:, 0:W].rearrange("p (h s) -> p h s", h=NG)
        hist = small_w[0:DEC_B * HIST, W:2 * W]
        wpl = small_w[:, 2 * W:3 * W].rearrange("p (g d) -> p g d", g=NG)
        bd_raw, bd = (small_w[0:NS, a:a + NG * NS].rearrange("p (h t) -> p h t", h=NG)
                      for a in (3 * W, 3 * W + NG * NS))
        psc = cols[:, 0:4]
        inv_n = cols[:, 4:68].rearrange("p (g n) -> p g n", g=NG)
        up_n = cols[:, 68:84]
        bst = cols[:, 84:84 + 6 * TILES].rearrange("p (t s) -> p t s", t=TILES)
        mv = cols[:, 84 + 6 * TILES:84 + 8 * TILES].rearrange("p (t s) -> p t s", t=TILES)
        ones = rows[0:1, 0:P]
        bsp = rows[0:1, P:P + NG * P].rearrange("p (h t) -> p h t", h=NG)
        bss = rows[0:1, P + NG * P:P + NG * (P + NS)]
        lgT = mixT[:, :, :].rearrange("p a b -> p (a b)")[0:NG + NE, 0:TILES * P]
        h_half = xg[0:NS, 0:BLOCK]
        hp_out = perm[0:HIST, 0].rearrange("p a b -> p (a b)")[:, 0:W]
        a_new = perm[:, 0, NG:KC, 0:NS]
        hs_out = perm[0:NS, 1].rearrange("p a b -> p (a b)")[:, 0:W]
        junk = win[:, :, :, :].rearrange("p a g n -> p (a g n)")[:, 0:TILES * D].rearrange(
            "p (t d) -> p t d", t=TILES)
        zp = ext[:, :, HIST:EXT_S]
        zs = ext[:, :, EXT_S:EXT].rearrange("p g (b n) -> p g b n", b=DEC_B)

        ple_bank = (0, 1, 2, 3, 2, 3)

        win_flat = win[:, :, :, :].rearrange("p a g n -> p (a g n)")
        n_sel = TILES * SLOTS * NE // 2
        memb = win_flat[:, 0:TILES * NE // 2].bitcast(BF16).rearrange("p (t e) -> p t e", t=TILES)
        at = 436
        place_b = win_flat[:, at:at + TILES * NE // 2].bitcast(BF16).rearrange("p (t e) -> p t e", t=TILES)
        at += TILES * NE // 2
        r_a, r_b = (win_flat[0:SLOTS, at + n * NE:at + (n + 1) * NE] for n in range(2))
        at += 2 * NE
        sel = win_flat[:, at:at + n_sel].bitcast(BF16).rearrange("p (t s e) -> p t s e", t=TILES, s=SLOTS)
        at += n_sel
        sel_s = win_flat[:, at:at + SLOTS * NE // 2].bitcast(BF16).rearrange("p (s e) -> p s e", s=SLOTS)
        ext_flat = ext[:, :, :].rearrange("p g n -> p (g n)")
        taken = [NG * EXT - 588]

        def take(n, parts=P):
            a = taken[0]
            taken[0] += n
            assert taken[0] <= NG * EXT
            return ext_flat[0:parts, a:a + n]

        def take_t(n):
            return take(TILES * n).rearrange("p (t n) -> p t n", t=TILES)

        grp, grp_x, grp_w = take_t(8), take_t(NG), take_t(NG)
        em, oh1, oh2, tmp = take_t(NE), take_t(NE), take_t(NE), take_t(NE)
        top, top_n, g_n = take_t(8), take_t(8), take_t(8)
        top_u, g_u = take_t(8).bitcast(U32), take_t(8).bitcast(U32)
        s_g, m_1, m_t, e_2 = (take_t(1) for _ in range(4))
        pen = take_t(NG)
        taken[0] += taken[0] % 2
        before, ones_b = low_ones[:, 0, :], low_ones[:, 1, :]
        tok_f = cols[:, 68:68 + 2 * TILES].rearrange("p (t c) -> p t c", t=TILES)

        ps = ctx.enter_context(nc.psum_tensor("ps", [P, 8, 512], F32))
        p_gu, p_t, p_y, p_x = ps[:, 0:2, :], ps[:, 2, :], ps[:, 3:5, :], ps[:, 5:7, :]
        IDX, FIRST_IDX, LOGITS, LOGIT_ROWS, PLACES = 7, 4, 6, 7, 5
        p_t = p_t[:, 0:2 * 4 * SLOTS].rearrange("p (g j s) -> p g j s", g=2, j=4)

        h_bank, hn_bank = (4, 2, 0), (6, 4, 2)

        def at_half(t, half):
            return slice(half * NS, half * NS + NS) if t == TILES - 1 else slice(0, P)

        def halves_by_chunk(t):
            order = [(half, k) for half in range(2) for k in range(KC)]
            return sorted(order, key=lambda x: x[1]) if t == TILES - 1 else order

        x_in = [sem(f"x_in{t}") for t in range(TILES)]
        g_row_in, p_in, small_in, row_in_s = sem("g_row_in"), sem("p_in"), sem("small_in"), sem("bias_in")
        setup_in, wpl_in = sem("setup_in"), sem("w_pool_in")
        gvb_in, bd_in = sem("gvb_in"), sem("bd_in")
        ple_in, last_in = sem("w_ple_in"), sem("last_half_in")
        raw_in = [sem(f"raw_in{s}") for s in range(RING)]
        ident_s, const_s, pool_c = sem("ident_ready"), sem("consts_ready"), sem("pool_chain")
        ws_masked, bd_ready = sem("ws_masked"), sem("bd_ready")
        vec_c, pass_c = sem("vector_chain"), sem("pass_chain")
        sq, ms, rt_s = sem("squares_summed"), sem("mean_squares"), sem("roots")
        normed, nT_s, nT_f = sem("rows_normed"), sem("normed_transposed"), sem("transposes_copied")
        pT_s, pT_f, ple_s, ple_f = sem("p_transposed"), sem("pT_copied"), sem("ple_done"), sem("ple_copied")
        ht_s, set_s = sem("hist_in_transposed"), sem("spatial_weights_transposed")
        hist_f, wsp_f = sem("hist_copied"), sem("spatial_weights_copied")
        a_s, a_f, v_s, v_f, u_s, u_f = (sem(n) for n in (
            "a_done", "a_copied", "v_done", "v_gelu", "u_done", "u_gelu"))
        v_ms, v_rt, v_n, v_out = sem("v_variance"), sem("v_root"), sem("v_normed"), sem("v_stored")
        hst_s, hst_f, hst_out = sem("hist_transposed"), sem("hist_rows_copied"), sem("hist_stored")
        pooled, pl_s, pl_f = sem("pooled"), sem("pool_mixed"), sem("pool_scaled")
        sp_s, sp_f, wo_s, h_s = sem("spatial_done"), sem("gated"), sem("w_out_done"), sem("h_ready")
        lgT_s, lgT_f, b_in = sem("logits_by_column"), sem("logits_biased"), sem("router_bias_in")
        hn_out, hist_kept = sem("hn_stored"), sem("hist_kept")
        lg_s, ge_s, e2_s, memb_s, pos_s = (sem(n) for n in (
            "logits_done", "group_exp", "second_exp", "members_ready", "places_done"))
        ex_in, ex2_in = sem("group_shifted"), sem("second_shifted")
        iota_s, sel_r, idx_s, rows_r, most_r = (sem(n) for n in (
            "slot_numbers", "selection_ready", "slots_picked", "slot_rows_ready", "most_ready"))
        pads, turns = sem("pads_zeroed"), sem("pool_turns")
        pass_done, scattered, experts_done = sem("pass_done"), sem("all_scattered"), sem("experts_done")
        hi_ready, lo_ready, unit_done = sem("hi_ready"), sem("lo_ready"), sem("unit_done")
        gu_copied, t_done, silu_done, h_step, hr_ready = (sem(n) for n in (
            "gate_up_copied", "gate_up_transposed", "silu_done", "hidden_step", "hidden_ready"))
        y_copied, y_added, y_scat = sem("y_copied"), sem("y_added"), sem("y_scattered")
        cur_in, cur_out, x_gath = sem("gather_rows_set"), sem("scatter_rows_set"), sem("x_gathered")
        x_done, xhi_done, xr_ready = sem("x_transposed"), sem("x_high"), sem("x_ready")
        scale2, half_f = sem("gate_scale"), sem("half_copied")
        moe_in = [[sem(f"moe_in{t}_{c}") for c in range(2)] for t in range(TILES)]
        gate_in, gl_in = sem("gate_in"), sem("last_gains_in")
        h2_s, sq2, ms2, rt2, nrm2 = (sem(n) for n in (
            "moe_added", "squares2", "mean_squares2", "roots2", "rows_gained"))
        tr2, cp2, gt_s, sig_s, h3_s, y_s, out_s = (sem(n) for n in (
            "transposed2", "copied2", "gate_done", "sigmoid_done", "h_final", "y_ready", "y_stored"))

        block = ctx.enter_context(nc.Block())

        def over_pass(eng, one_pass):
            one_pass(0)
            eng.wait_ge(most_r, 1)
            busiest = eng.value_load(most[0:1, 0:1], min_val=0, max_val=NT)
            with eng.If(busiest > SLOTS):
                with eng.Fori(1, PASSES) as q:
                    with eng.If(busiest > q * SLOTS):
                        one_pass(q)
            return busiest

        def over_rounds(eng, q, step):
            step(q * ROUNDS, 0, q, True, False)
            with eng.Fori(1, PAIRS) as i:
                step(q * ROUNDS + i, i, q, False, False)
            step(q * ROUNDS + PAIRS, PAIRS, q, False, True)

        def has(u, first, last):
            down_b = u // 2 == 2
            return down_b if last else not (first and down_b)

        def counted(u, first, last):
            return {(True, False, 3): 3, (False, True, 4): 5, (False, True, 5): 7}.get((first, last, u), 1)

        def wait_for_buffer(eng, n, u, last, size):
            if last:
                before = u + (UNITS - 1 - u) // size * size
                eng.wait_ge(unit_done, (n - 1) * UNITS + before + 1)
            elif not (isinstance(n, int) and n * UNITS + u < size):
                eng.wait_ge(unit_done, n * UNITS + u - size + 1)

        @block.sync
        def _(sp):
            for t, r in enumerate(ROWS):
                sp.dma_start(h[0:r, t, :], x_rows[t]).then_inc(x_in[t], 16)
                if t == 0:
                    sp.dma_start(g_row[:, :], g_mix.partition_broadcast(P).rearrange(
                        "q o d -> q (o d)")).then_inc(g_row_in, 16)
            for slot, part in enumerate((0, 2, 1)):
                sp.dma_start(ring[:, slot, :].rearrange("p (k n) -> p k n", k=KC),
                             w_in_v[:, :, part * W:(part + 1) * W]).then_inc(raw_in[slot], 16)
                if slot == 0:
                    for t, r in enumerate(ROWS):
                        sp.dma_start(p_tok[0:r, t, :], p_rows[t]).then_inc(p_in, 16)
                    sp.dma_start(hist, state_pool[0].rearrange("b r c -> (b r) c")).then_inc(setup_in, 16)
                    sp.dma_start(wsp, w_spatial[0].rearrange("h t s -> t h s")).then_inc(setup_in, 16)
            for s in range(2):
                sp.dma_start(ring[:, 3 + s, :].rearrange("p (k n) -> p k n", k=4),
                             w_out_v[:, 4 * s:4 * s + 4, :]).then_inc(raw_in[3 + s], 16)
            sp.dma_start(w_ple_sb[:, :, :], w_ple[0].rearrange("(p k) n -> p k n", k=2)).then_inc(ple_in, 16)
            sp.wait_ge(normed, 3)
            sp.dma_start(g_row[:, :], g_ffn.partition_broadcast(P).rearrange(
                "q o d -> q (o d)")).then_inc(g_row_in, 16)

            expert_w = [w_eg[0].rearrange("e (p k) n -> e p (k n)", k=KC),
                        w_eu[0].rearrange("e (p k) n -> e p (k n)", k=KC),
                        w_ed[0].rearrange("e (p j) n -> e p (j n)", j=4)]

            def load_round(n, i, q, first, last):
                for slot in range(RING):
                    if has(2 * slot, first, last):
                        sp.wait_ge(wo_s, 3)
                        sp.wait_ge(unit_done, (n - 1) * UNITS + 2 * slot + 2)
                        kind, of_b = ((0, 0), (1, 0), (2, -1), (0, 1), (1, 1), (2, 0))[slot]
                        src = expert_w[kind][bass.ds(i * 2 + of_b, 1), :, :].rearrange("o p n -> (o p) n")
                        if last:
                            cut = UBLOCKS * BLOCK
                            sp.dma_start(ring[:, slot, 0:cut], src[:, 0:cut]).then_inc(raw_in[slot], 16)
                            sp.dma_start(ring[:, slot, cut:], src[:, cut:]).then_inc(last_in, 16)
                        else:
                            sp.dma_start(ring[:, slot, :], src).then_inc(raw_in[slot], 16)

            def store_mixer():
                sp.wait_ge(hst_f, 2)
                sp.dma_start(new_pool_prompt[0, 0], hp_out).then_inc(hst_out, 16)
                sp.dma_start(new_pool_sample[0].rearrange("b r c -> b r c")[:, HIST - DEC_L:HIST, :],
                             hs_out).then_inc(hst_out, 16)
                sp.dma_start(new_pool_sample[0, :, 0:HIST - DEC_L, :],
                             state_pool[0, :, DEC_L:HIST, :]).then_inc(hist_kept, 16)
                sp.wait_ge(v_n, 3)
                sp.dma_start(new_vchunk[0].rearrange("b l w -> (b l) w"), vt[0:NS, 2, :]).then_inc(v_out, 16)

            def store_hn(t):
                sp.wait_ge(normed, 3 + t + 1)
                sp.dma_start(hn_rows[t * P:t * P + ROWS[t], :],
                             perm[0:ROWS[t], t].rearrange("p k q -> p (k q)")).then_inc(hn_out, 16)

            def first_round(n, i, q, first, last):
                for slot, tenant, count, kind, e in ((0, a_s, NG, 0, 0), (1, v_s, TILES, 1, 0),
                                                     (5, sp_s, 1, 2, 0), (3, wo_s, TILES, 0, 1),
                                                     (4, wo_s, TILES, 1, 1)):
                    sp.wait_ge(tenant, count)
                    sp.dma_start(ring[:, slot, :], expert_w[kind][e]).then_inc(raw_in[slot], 16)
                    if slot == 1:
                        store_mixer()
                    if slot == 5:
                        store_hn(0)
                        store_hn(1)
                    if slot == 3:
                        store_hn(2)

            def one_pass(q):
                def step(n, i, q, first, last):
                    (first_round if isinstance(n, int) and n == 0 else load_round)(n, i, q, first, last)
                over_rounds(sp, q, step)

            busiest = over_pass(sp, one_pass)
            with sp.If(busiest > SLOTS):
                sp.wait_ge(experts_done, 1)
                sp.wait_ge(scattered, 1)
            for s in range(2):
                sp.wait_ge(unit_done, UNITS * (PAIRS - 1) + 2 * (3 + s) + 2)
                sp.dma_start(ring[:, 3 + s, :], w_gate_v[:, 4 * D * s:4 * D * (s + 1)]).then_inc(gate_in, 16)
            sp.wait_ge(unit_done, UNITS * PAIRS)
            for c, g in enumerate((g_ple, g_final.rearrange("(o d) -> o d", o=1))):
                sp.dma_start(ring[:, 5, c * D:(c + 1) * D], g.partition_broadcast(P).rearrange(
                    "q o d -> q (o d)")).then_inc(gl_in, 16)
            sp.wait_ge(y_scat, 16 * NE)
            for t, r in enumerate(ROWS):
                for c in range(2):
                    sp.dma_start(ring[0:r, c, t * D:(t + 1) * D],
                                 moe_rows[c * NT + t * P:c * NT + t * P + r, :]).then_inc(moe_in[t][c], 16)
            for t, r in enumerate(ROWS):
                sp.wait_ge(y_s, t + 1)
                sp.dma_start(y_rows[t], ple[0:r, t, :]).then_inc(out_s, 16)
            sp.wait_ge(out_s, 16 * TILES)
            sp.wait_ge(hst_out, 32)
            sp.wait_ge(hist_kept, 16)
            sp.wait_ge(v_out, 16)

        @block.gpsimd
        def _(pool):
            link = chain(pool, pool_c)
            link(nc.gpsimd.memset(ident[:, :], 0.0))
            nc.gpsimd.affine_select(out=ident[:, :], in_=ident[:, :], compare_op=ALU.not_equal, fill=1.0,
                                    base=0, pattern=[[-1, P]], channel_multiplier=1).then_inc(ident_s, 1)
            link(nc.gpsimd.memset(bd_raw, 0.0))
            for b in range(DEC_B):
                pool.dma_start(bd_raw[DEC_L * b:DEC_L * (b + 1), :, DEC_L * b:DEC_L * (b + 1)],
                               w_spatial[0].rearrange("h t s -> t h s")[0:DEC_L, :, 0:DEC_L]).then_inc(bd_in, 16)
            link(nc.gpsimd.memset(fold[:, :], 0.0))
            for base in (0, -HALF):
                link(nc.gpsimd.affine_select(out=fold[:, :], in_=fold[:, :], compare_op=ALU.not_equal,
                                             fill=1.0, base=base, pattern=[[-1, SLOTS]],
                                             channel_multiplier=1))
            link(nc.gpsimd.memset(xg[:, :], 0.0))
            link(nc.gpsimd.iota(e_row[:, :], [[1, NE]], base=0, channel_multiplier=0,
                                allow_small_or_imprecise_dtypes=True))
            link(nc.gpsimd.iota(up_n, [[1, 16]], base=1, channel_multiplier=0,
                                allow_small_or_imprecise_dtypes=True))
            nc.gpsimd.memset(row_in[:, :], EMPTY).then_inc(const_s, 1)
            nc.gpsimd.memset(row_out[:, :], EMPTY).then_inc(const_s, 1)
            nc.gpsimd.memset(ones, 1.0).then_inc(const_s, 1)
            pool.wait_ge(wsp_f, 2)
            nc.gpsimd.affine_select(out=bd, in_=bd, compare_op=ALU.is_ge, fill=0.0, base=0,
                                    pattern=[[0, NG], [1, NS]], channel_multiplier=-1).then_inc(bd_ready, 1)
            pool.wait_ge(row_in_s, 16)
            nc.gpsimd.tensor_copy(
                bss.rearrange("p (h b l) -> p h b l", h=NG, b=DEC_B),
                bsp[:, :, 0:DEC_L].unsqueeze(2).to_broadcast([1, NG, DEC_B, DEC_L])).then_inc(bd_ready, 1)
            nc.gpsimd.affine_select(out=wsT[:, :, :], in_=wsT[:, :, :], compare_op=ALU.is_ge, fill=0.0,
                                    base=0, pattern=[[0, NG], [1, P]],
                                    channel_multiplier=-1).then_inc(ws_masked, 1)
            pool.wait_ge(pooled, NG + 1)
            pool.wait_ge(hst_s, 1)
            link(nc.gpsimd.memset(ones_b, 1.0))
            link(nc.gpsimd.iota(tok_f[:, :, 0], [[0, TILES]], base=0, channel_multiplier=1,
                                allow_small_or_imprecise_dtypes=True))
            link(nc.gpsimd.iota(tok_f[:, :, 1], [[P, TILES]], base=-EMPTY, channel_multiplier=0,
                                allow_small_or_imprecise_dtypes=True))
            link(nc.gpsimd.tensor_copy(tok[:, :, 0:2], tok_f))
            nc.gpsimd.affine_select(out=before, in_=ones_b, compare_op=ALU.is_gt, fill=0.0, base=0,
                                    pattern=[[1, P]], channel_multiplier=-1).then_inc(const_s, 1)

            def slot_numbers():
                nc.gpsimd.iota(sel_s, [[1, SLOTS], [0, NE]], base=0, channel_multiplier=0,
                               allow_small_or_imprecise_dtypes=True).then_inc(iota_s, 1)

            def gather(x, i):
                need(pool, x_done, x)
                pool.sem_inc(turns, 1)
                nc.gpsimd.tensor_copy(cur[:, 0:2], row_in[:, bass.ds(i * 2, 2)]).then_inc(cur_in, 1)
                pool.wait_ge(hn_out, 16 * TILES)
                pool.wait_ge(cur_in, x + 1)
                pool.sem_inc(turns, 1)
                for e in range(2):
                    nc.gpsimd.indirect_dma_start(
                        xg[e * SLOTS:(e + 1) * SLOTS, :], None, hn_rows,
                        bass.IndirectOffsetOnAxis(cur[:, e:e + 1].bitcast(U32), 0),
                        bounds_check=NT - 1, oob_is_err=False).then_inc(x_gath, 16)

            def scatter(x, i):
                need(pool, y_scat, x * 16)
                pool.sem_inc(turns, 1)
                nc.gpsimd.tensor_copy(cur[:, 2:3], row_out[:, bass.ds(i, 1)]).then_inc(cur_out, 1)
                pool.wait_ge(cur_out, x + 1)
                pool.wait_ge(y_added, x + 1)
                pool.sem_inc(turns, 1)
                nc.gpsimd.indirect_dma_start(
                    moe_rows, bass.IndirectOffsetOnAxis(cur[:, 2:3].bitcast(U32), 0), yo[:, :], None,
                    bounds_check=2 * NT - 1, oob_is_err=False).then_inc(y_scat, 16)

            def step(n, i, q, first, last):
                if first:
                    pool.wait_ge(rows_r, 2 * q + 2)
                    pool.sem_inc(turns, 1)
                if not last:
                    gather(n + 1, i + 1)
                if not first:
                    for e in range(2):
                        scatter((q * PAIRS + i) * 2 - 2 + e, i * 2 - 2 + e)

            def zero(*bufs):
                for buf in bufs:
                    for c in range(buf.shape[1]):
                        last = nc.gpsimd.memset(buf[:, c], 0.0)
                last.then_inc(pads, 1)

            def one_pass(q):
                if isinstance(q, int):
                    pool.wait_ge(normed, 6)
                slot_numbers()
                if isinstance(q, int):
                    pool.wait_ge(lg_s, 1)
                    zero(xr[:, :, :, :, SLOTS:HALF].bitcast(F32), xz[:, :, :, SLOTS:P],
                         h32[:, :, SLOTS:P], hr[:, :, :, SLOTS:HALF].bitcast(F32))
                pool.wait_ge(rows_r, 2 * q + 1)
                pool.sem_inc(turns, 1)
                gather(q * ROUNDS, 0)
                over_rounds(pool, q, step)
                pool.wait_ge(y_scat, (q + 1) * (16 * NE))
                pool.sem_inc(turns, 1)
                nc.gpsimd.memset(spare[:, 0:1], 0.0).then_inc(pass_done, 1)
                pool.wait_ge(pass_done, q + 1)
                pool.sem_inc(turns, 1)

            over_pass(pool, one_pass)
            nc.gpsimd.memset(spare[:, 0:1], 0.0).then_inc(scattered, 1)

        @block.tensor
        def _(pe):
            mm = nc.tensor.matmul

            def tr(out, in_):
                k = in_.shape[0]
                return nc.tensor.transpose(out, in_, ident[0:k, 0:k])

            pe.wait_ge(ident_s, 1)
            def transposes(t, r, bank, m):
                for k in range(KC):
                    last = tr(ps[:, bank + k // 4, (k % 4) * P:(k % 4) * P + m], perm[0:m, t, k, :])
                return last

            for t, r in enumerate(ROWS):
                pe.wait_ge(normed, t + 1)
                if t == 2:
                    pe.wait_ge(nT_f, 1)
                transposes(t, r, 4 + 2 * (t % 2), r).then_inc(nT_s, 1)
            w_a, w_v, w_u = (ring[:, s, :].rearrange("p (k n) -> p k n", k=KC) for s in range(3))
            pe.wait_ge(nT_f, 3)
            pe.wait_ge(raw_in[0], 16)
            for g in range(NG):
                for k in range(KC):
                    last = mm(ps[:, 4 + g, 0:NT], w_a[:, k, g * P:(g + 1) * P], nT[:, k, 0:NT],
                              start=k == 0, stop=k == KC - 1)
                last.then_inc(a_s, 1)
            pe.wait_ge(p_in, 16 * TILES)
            for t, r in enumerate(ROWS):
                for k in range(2):
                    n = 2 * t + k
                    last = tr(ps[:, n // 4, (n % 4) * P:(n % 4) * P + r],
                              p_tok[0:r, t, :].rearrange("p (q k) -> p k q", k=2)[:, k, :])
            last.then_inc(pT_s, 1)
            pe.wait_ge(setup_in, 32)
            for g in range(NG):
                last = tr(ps[:, 2, g * P:g * P + DEC_B * HIST], hist[:, g * P:(g + 1) * P])
            last.then_inc(ht_s, 1)
            for g in range(NG):
                last = tr(ps[:, 3, g * P:(g + 1) * P], wsp[:, g, :])
            last.then_inc(set_s, 1)
            pe.wait_ge(raw_in[1], 16)
            pe.wait_ge(pT_f, 1)
            pe.wait_ge(hist_f, 1)
            for t, r in enumerate(ROWS):
                for k in range(KC):
                    for half in range(2 if t == TILES - 1 else 1):
                        cols_v = slice(half * W // 2, half * W // 2 + W // 2) if t == TILES - 1 else slice(0, W)
                        last = mm(ps[at_half(t, half), t, cols_v], nT[:, k, t * P:t * P + r],
                                  w_v[:, k, cols_v], start=k == 0, stop=k == KC - 1)
                last.then_inc(v_s, 1)
            pe.wait_ge(bd_in, 16 * DEC_B)
            pe.wait_ge(a_f, NG)
            for g in range(NG):
                last = tr(ps[0:NS, 7, g * NS:(g + 1) * NS], bd_raw[:, g, :])
            last.then_inc(set_s, 1)
            pe.wait_ge(raw_in[2], 16)
            pe.wait_ge(wsp_f, 1)
            for g in range(NG):
                if g:
                    pe.wait_ge(a_f, g)
                for k in range(KC):
                    last = mm(ps[:, 3 + g, 0:NT], w_u[:, k, g * P:(g + 1) * P], nT[:, k, 0:NT],
                              start=k == 0, stop=k == KC - 1)
                last.then_inc(u_s, 1)
            pe.wait_ge(wsp_f, 2)
            pe.wait_ge(v_f, 3)
            for g in range(NG):
                tr(ps[0:HIST, 7, g * P:(g + 1) * P], ext[:, g, EXT_S - HIST:EXT_S])
            for g in range(NG):
                last = tr(ps[0:NS, 2, g * P:(g + 1) * P], a_new[:, g, :])
            last.then_inc(hst_s, 1)
            pe.wait_ge(wpl_in, 16)
            pe.wait_ge(pooled, NG)
            pe.wait_ge(u_f, NG)
            pe.wait_ge(hst_f, 1)
            for g in range(NG):
                mm(ps[:, 4 + g, 0:NT], wpl[:, g, :], mixT[:, g, :], start=True, stop=True).then_inc(pl_s, 1)
            pe.wait_ge(v_n, 3)
            pe.wait_ge(ws_masked, 1)
            pe.wait_ge(bd_ready, 2)
            pe.wait_ge(const_s, 3)
            pe.wait_ge(row_in_s, 16)
            pe.wait_ge(u_f, 1)
            for g in range(NG):
                for c in range(2):
                    out = ps[:, g // 2, (g % 2) * SEQ + c * P:(g % 2) * SEQ + (c + 1) * P]
                    mm(out, vt[:, c, g * P:(g + 1) * P], wsT[:, g, :], start=True, stop=False)
                    mm(out, ones, bsp[:, g, :], start=False, stop=True)
                out = ps[:, 3, g * NS:(g + 1) * NS]
                mm(out, vt[0:NS, 2, g * P:(g + 1) * P], bd[:, g, :], start=True, stop=False)
                last = mm(out, ones, bss[:, g * NS:(g + 1) * NS], start=False, stop=True)
            last.then_inc(sp_s, 1)
            pe.wait_ge(raw_in[3], 16)
            pe.wait_ge(raw_in[4], 16)
            pe.wait_ge(pl_f, NG)
            pe.wait_ge(hst_f, 2)
            def w_out_product(t, r):
                order = halves_by_chunk(t)
                if t == 0:
                    order.sort(key=lambda x: x[1] // NG)
                for n, (half, k) in enumerate(order):
                    if t == 0 and n == KC:
                        pe.wait_ge(sp_f, 2)
                    w = ring[:, 3 + k // 4, (k % 4) * D + half * BLOCK:(k % 4) * D + (half + 1) * BLOCK]
                    last = mm(ps[at_half(t, half), h_bank[t] + half, :], mixT[:, k, t * P:t * P + r], w,
                              start=k == 0, stop=k == KC - 1)
                last.then_inc(wo_s, 1)

            def turn_hn(t, r):
                pe.wait_ge(normed, 3 + t + 1)
                transposes(t, r, hn_bank[t], r).then_inc(nT_s, 1)

            def logits(t, r):
                pe.wait_ge(nT_f, 3 + t + 1)
                for k in range(KC):
                    last = mm(ps[0:NG + NE, LOGITS, t * P:t * P + r], rt[:, k, :], nT[:, k, t * P:t * P + r],
                              start=k == 0, stop=k == KC - 1)
                last.then_inc(lgT_s, 1)

            w_out_product(0, P)
            w_out_product(1, P)
            turn_hn(0, P)
            w_out_product(2, NS)
            turn_hn(1, P)
            pe.wait_ge(small_in, 48)
            logits(0, P)
            logits(1, P)
            turn_hn(2, NS)
            logits(2, NS)
            pe.wait_ge(lgT_f, 1)
            for t in range(TILES):
                last = tr(ps[:, LOGIT_ROWS, t * (NG + NE):(t + 1) * (NG + NE)], lgT[:, t * P:(t + 1) * P])
            last.then_inc(lg_s, 1)
            def ple_product(n):
                t, half = n // 2, n % 2
                if n == 0:
                    pe.wait_ge(ple_in, 16)
                    pe.wait_ge(nT_f, 6)
                need(pe, ple_f, n - 1 if n > 3 else 0)
                for k in range(2):
                    done = mm(ps[0:ROWS[t], ple_bank[n], :], pT[:, k, t * P:t * P + ROWS[t]],
                              w_ple_sb[:, k, half * BLOCK:(half + 1) * BLOCK], start=k == 0, stop=k == 1)
                done.then_inc(ple_s, 1)

            ple_product(0)
            pe.wait_ge(memb_s, 1)
            pe.wait_ge(const_s, 4)
            for t in range(TILES):
                for c in range(t + 1):
                    mm(ps[:, PLACES, t * NE:(t + 1) * NE], before if c == t else ones_b, memb[:, c, :],
                       start=c == 0, stop=c == t)
            for c in range(TILES):
                last = mm(ps[:, PLACES, TILES * NE:(TILES + 1) * NE], ones_b, memb[:, c, :],
                          start=c == 0, stop=c == TILES - 1)
            last.then_inc(pos_s, 1)

            def pick_slots(q, n):
                bank, experts_n = ((FIRST_IDX, 2), (IDX, NE))[n]
                pe.wait_ge(sel_r, 2 * q + n + 1)
                for e in range(experts_n):
                    for t in range(TILES):
                        last = mm(ps[0:SLOTS, bank, 3 * e:3 * e + 3], sel[:, t, :, e], tok[:, t, :],
                                  start=t == 0, stop=t == TILES - 1)
                last.then_inc(idx_s, 1)

            def turn_x(x):
                pe.wait_ge(x_gath, (x + 1) * 32)
                for k in range(KC):
                    last = tr(p_x[:, k // 4, (k % 4) * P:(k % 4) * P + 2 * SLOTS],
                              xg[:, k * P:(k + 1) * P])
                last.then_inc(x_done, 1)

            def multiply(n, u, first, last):
                pe.wait_ge(lo_ready, n * UNITS + u + 1)
                slot, e, down = u // 2, u // 6, u % 6 >= 4
                for b in range(UBLOCKS):
                    blk = (u % 2) * UBLOCKS + b
                    if down:
                        out, z = p_y[:, blk % 2, :], h32[:, blk // 2, :]
                        parts = hr[:, blk // 2, :, :].rearrange("p a s -> p (a s)")
                        begin, end = blk < 2, blk >= MBLOCKS - 2
                    else:
                        out, z = p_gu[:, slot % 3, :], xz[:, u % 2, e, :]
                        parts = xr[:, blk, e, :, :].rearrange("p a s -> p (a s)")
                        begin, end = blk == 0, blk == MBLOCKS - 1
                    cut = slice(b * BLOCK, (b + 1) * BLOCK)
                    if b < SBLOCKS:
                        mm(out, parts, hi[:, u % HI_RING, cut], start=begin, stop=False)
                        done = mm(out, parts, lo[:, u % LO_RING, cut], start=False, stop=end)
                    else:
                        done = mm(out, z, ring[:, slot, blk * BLOCK:(blk + 1) * BLOCK],
                                  start=begin, stop=end)
                done.then_inc(unit_done, counted(u, first, last))

            def turn_hidden(x):
                if isinstance(x, int) and x == 0:
                    pe.wait_ge(ple_f, 6)
                pe.wait_ge(gu_copied, 2 * x + 2)
                need(pe, hr_ready, x)
                for c in range(2):
                    for j in range(4):
                        done = mm(p_t[:, c, j, :], gu[:, c, j, :], fold[:, :], start=True, stop=True)
                done.then_inc(t_done, 1)

            def step(n, i, q, first, last):
                x = (q * PAIRS + i) * 2
                if not last:
                    pe.wait_ge(xr_ready, q * PAIRS + i + 1)
                for u in range(UNITS):
                    if not has(u, first, last):
                        continue
                    if u == 4:
                        pe.wait_ge(hr_ready, x)
                        pe.wait_ge(y_added, x - 1)
                    if u == 10:
                        turn_x(n + 1)
                        pe.wait_ge(hr_ready, x + 1)
                        need(pe, y_added, x)
                    if not last and u == 6:
                        turn_hidden(x)
                    multiply(n, u, first, last)
                    if first and u == 3:
                        pick_slots(q, 1)
                if not last:
                    turn_hidden(x + 1)

            def one_pass(q):
                pick_slots(q, 0)
                if isinstance(q, int):
                    for n in (1, 2, 3):
                        ple_product(n)
                pe.wait_ge(most_r, 1)
                turn_x(q * ROUNDS)
                if isinstance(q, int):
                    ple_product(4)
                    ple_product(5)
                pe.wait_ge(pads, 1)
                over_rounds(pe, q, step)

            over_pass(pe, one_pass)

            def turn_rows(t, r):
                pe.wait_ge(nrm2, t + 1)
                need(pe, cp2, t)
                transposes(t, r, 6, r).then_inc(tr2, 1)

            pe.wait_ge(gate_in, 32)
            pe.wait_ge(moe_in[0][0], 16)
            for _ in range(2):
                mm(ps[:, 5, :], ident[:, :], w_ple_sb[:, 0, 0:BLOCK], start=True, stop=True)
            turn_rows(0, P)
            for t, r in enumerate(ROWS):
                pe.wait_ge(cp2, t + 1)
                for half, k in halves_by_chunk(t):
                    w = ring[:, 3 + k // 4, (k % 4) * D + half * BLOCK:(k % 4) * D + (half + 1) * BLOCK]
                    done = mm(ps[at_half(t, half), 2 * t + half, :], nT[:, k, t * P:t * P + r], w,
                              start=k == 0, stop=k == KC - 1)
                    if k == KC - 1:
                        done.then_inc(gt_s, 1)
                        if half == 0 and t < TILES - 1:
                            turn_rows(t + 1, ROWS[t + 1])

        @block.scalar
        def _(act):
            acti = nc.scalar.activation
            def norm(t, r, col, s_sq, s_ms, s_rt, base):
                acti(junk[0:r, t, :], h[0:r, t, :], ACT.Square,
                     accum_out=stat[0:r, col, t:t + 1]).then_inc(s_sq, 1)
                act.wait_ge(s_ms, base + t + 1)
                acti(stat[0:r, col + 2, t:t + 1], stat[0:r, col + 1, t:t + 1], ACT.Sqrt).then_inc(s_rt, 1)

            act.wait_ge(vec_c, 1)
            for t, r in enumerate(ROWS):
                act.wait_ge(x_in[t], 16)
                norm(t, r, 0, sq, ms, rt_s, 0)
            act.dma_start(wpl, w_pool[0].rearrange("g c d -> c g d")).then_inc(wpl_in, 16)
            act.dma_start(bsp, b_spatial).then_inc(row_in_s, 16)
            act.dma_start(b_col[0:NG, :], b_rg.rearrange("o n -> n o")).then_inc(b_in, 16)
            act.dma_start(b_col[NG:NG + NE, :], b_re.rearrange("o n -> n o")).then_inc(b_in, 16)
            act.dma_start(gv_row, g_v.partition_broadcast(P).rearrange("q o d -> q (o d)")).then_inc(gvb_in, 16)
            act.dma_start(bv_row, b_v.partition_broadcast(P).rearrange("q o d -> q (o d)")).then_inc(gvb_in, 16)
            act.dma_start(rt[:, :, 0:NG], w_rg[0].rearrange("(p k) n -> p k n", k=KC)).then_inc(small_in, 16)
            act.dma_start(rt[:, :, NG:NG + NE], w_re[0].rearrange("(p k) n -> p k n", k=KC)).then_inc(small_in, 16)
            act.dma_start(psc, pool_scale[0].rearrange("(g p) -> p g", p=P)).then_inc(small_in, 16)
            act.wait_ge(set_s, 1)
            acti(wsT[:, :, :], ps[:, 3, :].rearrange("p (h t) -> p h t", h=NG), ACT.Copy).then_inc(wsp_f, 1)
            for t, r in enumerate(ROWS):
                act.wait_ge(v_s, t + 1)
                if t < TILES - 1:
                    acti(vt[0:r, t, :], ps[0:r, t, :], ACT.Gelu_apprx_tanh).then_inc(v_f, 1)
                else:
                    for half in range(2):
                        cut = slice(half * W // 2, half * W // 2 + W // 2)
                        last = acti(vt[0:r, t, cut], ps[at_half(t, half), t, cut], ACT.Gelu_apprx_tanh)
                    last.then_inc(v_f, 1)
            act.wait_ge(set_s, 2)
            acti(bd, ps[0:NS, 7, 0:NG * NS].rearrange("p (h t) -> p h t", h=NG), ACT.Copy).then_inc(wsp_f, 1)
            act.wait_ge(v_ms, 3)
            acti(stat[:, 6, :], stat[:, 5, :], ACT.Sqrt).then_inc(v_rt, 1)
            for g in range(NG):
                act.wait_ge(u_s, g + 1)
                if g == 0:
                    act.wait_ge(pT_s, 1)
                acti(mixT[:, NG + g, :], ps[:, 3 + g, 0:NT], ACT.Gelu_apprx_tanh).then_inc(u_f, 1)
            act.wait_ge(small_in, 48)
            for g in range(NG):
                act.wait_ge(pl_s, g + 1)
                acti(mixT[:, g, :], ps[:, 4 + g, 0:NT], ACT.Copy, scale=psc[:, g:g + 1]).then_inc(pl_f, 1)
            for t, r in enumerate(ROWS):
                if t == TILES - 1:
                    act.wait_ge(wo_s, TILES)
                    acti(h_half, ps[at_half(t, 1), h_bank[t] + 1, :], ACT.Copy).then_inc(half_f, 1)
                act.wait_ge(h_s, t + 1)
                norm(t, r, 8, sq, ms, rt_s, 3)
            act.wait_ge(ex_in, 1)
            acti(grp_w[:, :, :], grp_x[:, :, :], ACT.Exp).then_inc(ge_s, 1)
            act.wait_ge(ex2_in, 1)
            acti(e_2[:, :, :], m_t[:, :, :], ACT.Exp).then_inc(e2_s, 1)

            def copy_ple(n):
                t, half = n // 2, n % 2
                act.wait_ge(ple_s, n + 1)
                acti(ple[0:ROWS[t], t, half * BLOCK:(half + 1) * BLOCK], ps[0:ROWS[t], ple_bank[n], :],
                     ACT.Copy).then_inc(ple_f, 1)

            def high_x(n):
                act.wait_ge(x_done, n + 1)
                for e in range(2):
                    last = acti(xr[:, :, e, 0, 0:SLOTS],
                                p_x.rearrange("p b (k s) -> p (b k) s", s=P)[:, :, e * SLOTS:(e + 1) * SLOTS],
                                ACT.Copy)
                last.then_inc(xhi_done, 1)

            def copy_y(x, units):
                act.wait_ge(unit_done, units)
                need(act, y_added, x)
                acti(yc[:, :].rearrange("p (b n) -> p b n", b=2), p_y[HALF:HALF + SLOTS, :, :],
                     ACT.Copy).then_inc(y_copied, 1)

            def high_w(n, i, q, u, first, last):
                if u % 2 == 0:
                    act.wait_ge(raw_in[u // 2], (q * PAIRS + i) * 16 + (16 if u in (4, 10) else 32))
                elif last:
                    act.wait_ge(last_in, q * 16 + 16)
                wait_for_buffer(act, n, u, last, HI_RING)
                off = (u % 2) * UBLOCKS * BLOCK
                acti(hi[:, u % HI_RING, :], ring[:, u // 2, off:off + SPLIT],
                     ACT.Copy).then_inc(hi_ready, counted(u, first, last))

            def copy_gu(n, x, u):
                c = (u % 6) // 2
                act.wait_ge(unit_done, n * UNITS + u + 1)
                if c == 0:
                    need(act, t_done, x)
                acti(gu[:, c, :, :].rearrange("p j q -> p q j"),
                     p_gu[:, c, :].rearrange("p (q j) -> p q j", j=4), ACT.Copy).then_inc(gu_copied, 1)

            def silu(x):
                act.wait_ge(t_done, x + 1)
                need(act, hr_ready, x)
                acti(sg[:, :, :], p_t[:, 0], ACT.Silu).then_inc(silu_done, 1)

            def step(n, i, q, first, last):
                x = (q * PAIRS + i) * 2

                def high(*units):
                    for u in units:
                        high_w(n, i, q, u, first, last)

                if not first:
                    copy_gu(n - 1, x - 1, 9)
                if last:
                    high(4, 5)
                if isinstance(n, int) and n == 0:
                    act.wait_ge(hn_out, 16 * TILES)
                    act.wait_ge(lg_s, 1)
                    high(0)
                    copy_ple(0)
                    high(1)
                    for m in (1, 2, 3):
                        copy_ple(m)
                    act.wait_ge(pads, 1)
                    high_x(n)
                    copy_ple(4)
                    copy_ple(5)
                    high(2)
                elif not last:
                    high_x(n)
                    high(0, 1, 2)
                if not first:
                    copy_y(x - 2, (n - 1) * UNITS + 12)
                if not last:
                    high(3)
                if not first:
                    silu(x - 1)
                if not (first or last):
                    high(4, 5)
                if not last:
                    copy_gu(n, x, 1)
                    high(6, 7)
                    copy_gu(n, x, 3)
                    high(8, 9)
                if not first:
                    copy_y(x - 1, n * UNITS + 6)
                if not last:
                    high(10)
                    silu(x)
                    high(11)
                    copy_gu(n, x + 1, 7)

            def one_pass(q):
                over_rounds(act, q, step)

            over_pass(act, one_pass)

            for t, r in enumerate(ROWS):
                act.wait_ge(h2_s, 2 * t + 2)
                norm(t, r, 0, sq2, ms2, rt2, 0)
            for t, r in enumerate(ROWS):
                act.wait_ge(scale2, t + 1)
                sig = (mixT[0:r, :, :].rearrange("p a b -> p (a b)") if t != 1 else win_flat[0:r, :])[:, 0:D]
                for half in range(2):
                    act.wait_ge(gt_s, 2 * t + half + 1)
                    rows_t = at_half(t, half)
                    acti(sig[:, half * BLOCK:(half + 1) * BLOCK], ps[rows_t, 2 * t + half, :], ACT.Sigmoid,
                         scale=stat[rows_t, 3, t:t + 1]).then_inc(sig_s, 1)
                acti(stat[0:1, 13, t:t + 1], stat[0:1, 14, t:t + 1], ACT.Sqrt)
                act.wait_ge(h3_s, 2 * t + 2)
                acti(ext_flat[0:r, 0:D], h[0:r, t, :], ACT.Square,
                     accum_out=stat[0:r, 8, t:t + 1]).then_inc(sq2, 1)
                act.wait_ge(ms2, 3 + t + 1)
                acti(stat[0:r, 10, t:t + 1], stat[0:r, 9, t:t + 1], ACT.Sqrt).then_inc(rt2, 1)

        @block.vector
        def _(dve):
            V = nc.vector
            link = chain(dve, vec_c)

            def mean_square(t, r, col, s_sq, s_ms, base):
                dve.wait_ge(s_sq, base + t + 1)
                V.tensor_scalar(stat[0:r, col + 1, t:t + 1], stat[0:r, col, t:t + 1], 1.0 / D, EPS,
                                ALU.mult, ALU.add).then_inc(s_ms, 1)

            def norm_rows(t, r, col, s_sq, s_ms, s_rt, base, gain, out, done):
                mean_square(t, r, col, s_sq, s_ms, base)
                dve.wait_ge(s_rt, base + t + 1)
                link(V.reciprocal(stat[0:r, col + 3, t:t + 1], stat[0:r, col + 2, t:t + 1]))
                src, g = h[0:r, t, :], gain[0:r]
                if out is None:
                    out = perm[0:r, t].rearrange("p k q -> p q k")
                    src = src.rearrange("p (q k) -> p q k", k=KC)
                    g = g.rearrange("p (q k) -> p q k", k=KC)
                V.scalar_tensor_tensor(out=out, in0=src, scalar=stat[0:r, col + 3, t:t + 1], in1=g,
                                       op0=ALU.mult, op1=ALU.mult).then_inc(done, 1)

            def copy_turned(t, m, bank):
                V.tensor_copy(nT[:, :, t * P:t * P + m],
                              ps[:, bank:bank + 2, :].rearrange("p b (k s) -> p (b k) s", s=P)[:, :, 0:m]
                              ).then_inc(nT_f, 1)

            link(V.memset(stat[:, :, :], 1.0))
            link(V.memset(ext[:, :, 0:HIST], 0.0))
            dve.wait_ge(g_row_in, 16)
            for t, r in enumerate(ROWS):
                norm_rows(t, r, 0, sq, ms, rt_s, 0, g_row, None, normed)
            for t, r in enumerate(ROWS):
                dve.wait_ge(nT_s, t + 1)
                copy_turned(t, r, 4 + 2 * (t % 2))
            dve.wait_ge(const_s, 3)
            for g in range(NG):
                last = V.tensor_scalar(inv_n[:, g, :], up_n, float(2 << g), None, ALU.min)
            link(last)
            link(V.reciprocal(inv_n, inv_n))
            for g in range(NG):
                dve.wait_ge(a_s, g + 1)
                V.tensor_copy(zp[:, g, :], ps[:, 4 + g, 0:SEQ])
                V.tensor_copy(a_new[:, g, :], ps[:, 4 + g, SEQ:NT])
                V.tensor_copy(zs[:, g, :, HIST:EXT_B],
                              ps[:, 4 + g, SEQ:NT].rearrange("p (b l) -> p b l", b=DEC_B)).then_inc(a_f, 1)
            dve.wait_ge(pT_s, 1)
            for k in range(2):
                for t, r in enumerate(ROWS):
                    n = 2 * t + k
                    last = V.tensor_copy(pT[:, k, t * P:t * P + r], ps[:, n // 4, (n % 4) * P:(n % 4) * P + r])
            last.then_inc(pT_f, 1)
            dve.wait_ge(ht_s, 1)
            for g in range(NG):
                last = V.tensor_copy(zs[:, g, :, 0:HIST],
                                     ps[:, 2, g * P:g * P + DEC_B * HIST].rearrange("p (b r) -> p b r", b=DEC_B))
            last.then_inc(hist_f, 1)
            dve.wait_ge(hist_f, 1)
            src = ext
            for w in range(NG):
                d, dst = 1 << w, win[:, w % 2]
                a = 2 * d - 1
                link(V.tensor_tensor(dst[:, w:NG, a:EXT], src[:, w:NG, a:EXT], src[:, w:NG, a - d:EXT - d],
                                     ALU.add))
                src = dst
            for g in range(NG):
                s = win[:, g % 2, g, :]
                V.scalar_tensor_tensor(out=mixT[:, g, 0:SEQ], in0=s[:, HIST:EXT_S], scalar=1.0 / (2 << g),
                                       in1=zp[:, g, :], op0=ALU.mult, op1=ALU.subtract)
                link(V.scalar_tensor_tensor(
                    out=mixT[:, g, SEQ:NT].rearrange("p (b l) -> p b l", b=DEC_B),
                    in0=s[:, EXT_S:EXT].rearrange("p (b n) -> p b n", b=DEC_B)[:, :, HIST:EXT_B],
                    scalar=1.0 / (2 << g), in1=zs[:, g, :, HIST:EXT_B], op0=ALU.mult, op1=ALU.subtract))
                link(V.tensor_tensor(mixT[:, g, 0:16], s[:, HIST:HIST + 16], inv_n[:, g, :], ALU.mult))
                V.tensor_tensor(mixT[:, g, 0:16], mixT[:, g, 0:16], zp[:, g, 0:16],
                                ALU.subtract).then_inc(pooled, 1)
            for t, r in enumerate(ROWS):
                dve.wait_ge(v_f, t + 1)
                link(V.bn_stats(bst[0:r, t, :], vt[0:r, t, :]))
                link(V.bn_aggr(mv[0:r, t, :], bst[0:r, t, :]))
                V.tensor_scalar(stat[0:r, 5, t:t + 1], mv[0:r, t, 1:2], EPS, None, ALU.add).then_inc(v_ms, 1)
            dve.wait_ge(v_rt, 1)
            link(V.reciprocal(stat[:, 7, :], stat[:, 6, :]))
            dve.wait_ge(gvb_in, 32)
            for t, r in enumerate(ROWS):
                link(V.tensor_scalar(vt[0:r, t, :], vt[0:r, t, :], mv[0:r, t, 0:1], stat[0:r, 7, t:t + 1],
                                     ALU.subtract, ALU.mult))
                link(V.tensor_tensor(vt[0:r, t, :], vt[0:r, t, :], gv_row[0:r], ALU.mult))
                V.tensor_tensor(vt[0:r, t, :], vt[0:r, t, :], bv_row[0:r], ALU.add).then_inc(v_n, 1)
            dve.wait_ge(hst_s, 1)
            V.tensor_copy(hp_out, ps[0:HIST, 7, :]).then_inc(hst_f, 1)
            V.tensor_copy(hs_out, ps[0:NS, 2, :]).then_inc(hst_f, 1)
            V.memset(stat[:, 15, :], 1.0).then_inc(pooled, 1)
            dve.wait_ge(sp_s, 1)
            dve.wait_ge(u_f, NG)
            V.tensor_tensor(mixT[:, NG:KC, 0:SEQ], mixT[:, NG:KC, 0:SEQ],
                            ps[:, 0:2, :].rearrange("p b (g s) -> p (b g) s", g=2), ALU.mult).then_inc(sp_f, 1)
            V.tensor_tensor(mixT[:, NG:KC, SEQ:NT], mixT[:, NG:KC, SEQ:NT],
                            ps[:, 3, 0:NG * NS].rearrange("p (g s) -> p g s", g=NG), ALU.mult).then_inc(sp_f, 1)
            dve.wait_ge(hst_out, 32)
            dve.wait_ge(g_row_in, 32)
            for t, r in enumerate(ROWS):
                dve.wait_ge(wo_s, t + 1)
                if t < TILES - 1:
                    V.tensor_tensor(h[0:r, t, :].rearrange("p (b n) -> p b n", b=2),
                                    h[0:r, t, :].rearrange("p (b n) -> p b n", b=2),
                                    ps[0:r, h_bank[t]:h_bank[t] + 2, :], ALU.add).then_inc(h_s, 1)
                else:
                    V.tensor_tensor(h[0:r, t, 0:BLOCK], h[0:r, t, 0:BLOCK], ps[0:r, h_bank[t], :], ALU.add)
                    dve.wait_ge(half_f, 1)
                    V.tensor_tensor(h[0:r, t, BLOCK:D], h[0:r, t, BLOCK:D], h_half, ALU.add).then_inc(h_s, 1)
                if t:
                    dve.wait_ge(nT_s, 3 + t)
                    copy_turned(t - 1, P, hn_bank[t - 1])
                norm_rows(t, r, 8, sq, ms, rt_s, 3, g_row, None, normed)
            V.memset(lgT[:, NT:TILES * P], 0.0)
            dve.wait_ge(nT_s, 6)
            copy_turned(2, NS, hn_bank[2])
            dve.wait_ge(lgT_s, TILES)
            dve.wait_ge(b_in, 32)
            V.tensor_scalar(lgT[:, 0:NT], ps[0:NG + NE, LOGITS, 0:NT], b_col[:, :], None,
                            ALU.add).then_inc(lgT_f, 1)

            def bc(a, n):
                return a.to_broadcast([P, TILES, n])

            def groups(a):
                return a.rearrange("p t (g e) -> p t g e", g=NG)

            numbers = e_row[:, :].unsqueeze(1).to_broadcast([P, TILES, NE])
            link(V.memset(grp[:, :, NG:8], -BIG))
            dve.wait_ge(const_s, 4)
            dve.wait_ge(lg_s, 1)
            out = ps[:, LOGIT_ROWS, 0:TILES * (NG + NE)].rearrange("p (t n) -> p t n", t=TILES)
            lg, le = out[:, :, 0:NG], out[:, :, NG:NG + NE]
            link(V.tensor_copy(grp[:, :, 0:NG], lg))
            for t in range(TILES):
                last = V.max(out=top[:, t, :], in_=grp[:, t, :])
            link(last)
            for t in range(TILES):
                last = V.max_index(g_u[:, t, :], top[:, t, :], grp[:, t, :])
            link(last)
            V.tensor_tensor(grp_x, grp[:, :, 0:NG], bc(top[:, :, 0:1], NG), ALU.subtract).then_inc(ex_in, 1)
            link(V.tensor_copy(g_n, g_u))
            link(V.tensor_tensor(pen, numbers[:, :, 0:NG], bc(g_n[:, :, 0:1], NG), ALU.is_equal))
            link(V.tensor_scalar(pen, pen, -1.0, BIG, ALU.add, ALU.mult))
            for t in range(TILES):
                last = V.tensor_tensor(groups(em)[:, t], groups(le)[:, t],
                                       pen[:, t, :].unsqueeze(2).to_broadcast([P, NG, NE // NG]), ALU.add)
            link(last)
            for t in range(TILES):
                last = V.max(out=top[:, t, :], in_=em[:, t, :])
            link(last)
            for t in range(TILES):
                last = V.max_index(top_u[:, t, :], top[:, t, :], em[:, t, :])
            link(last)
            V.tensor_tensor(m_t, top[:, :, 1:2], top[:, :, 0:1], ALU.subtract).then_inc(ex2_in, 1)
            link(V.tensor_copy(top_n, top_u))
            V.tensor_tensor(oh1, numbers, bc(top_n[:, :, 0:1], NE), ALU.is_equal)
            link(V.tensor_tensor(oh2, numbers, bc(top_n[:, :, 1:2], NE), ALU.is_equal))
            link(V.tensor_tensor(memb, oh1, oh2, ALU.add))
            V.memset(memb[NS:P, 2, :], 0.0).then_inc(memb_s, 1)
            dve.wait_ge(memb_s, 1)
            link(V.tensor_scalar(tmp, memb, -NOWHERE, NOWHERE, ALU.mult, ALU.add))
            link(V.tensor_copy(tok[:, :, 2:3], top_n[:, :, 1:2]))
            dve.wait_ge(pos_s, 1)
            link(V.tensor_tensor(place[:, :, :], tmp,
                                 ps[:, PLACES, 0:TILES * NE].rearrange("p (t e) -> p t e", t=TILES), ALU.add))

            def choose(e_end):
                for t in range(TILES):
                    last = V.tensor_tensor(
                        sel[:, t, :, 0:e_end], sel_s[:, :, 0:e_end],
                        place_b[:, t, 0:e_end].unsqueeze(1).to_broadcast([P, SLOTS, e_end]), ALU.is_equal)
                last.then_inc(sel_r, 1)

            def first_slots(q, step):
                dve.wait_ge(iota_s, q + 1)
                step(V.tensor_copy(place_b, place[:, :, :]))
                choose(2)
                dve.wait_ge(idx_s, 2 * q + 1)
                out = ps[0:SLOTS, FIRST_IDX, 0:6].rearrange("p (e c) -> p e c", c=3)
                step(V.tensor_scalar(r_a[:, 0:2], out[:, :, 0], float(EMPTY), None, ALU.add))
                V.tensor_tensor(row_in[:, 0:2], r_a[:, 0:2], out[:, :, 1], ALU.add).then_inc(rows_r, 1)

            def all_slots(q, step):
                dve.wait_ge(idx_s, 2 * q + 2)
                dve.wait_ge(cur_in, q * ROUNDS + 1)
                out = ps[0:SLOTS, IDX, 0:3 * NE].rearrange("p (e c) -> p e c", c=3)
                step(V.tensor_scalar(r_a, out[:, :, 0], float(EMPTY), None, ALU.add))
                step(V.tensor_tensor(r_a, r_a, out[:, :, 1], ALU.add))
                step(V.tensor_tensor(r_b, out[:, :, 2], e_row[0:SLOTS, :], ALU.is_equal))
                V.tensor_copy(row_in[:, 0:NE], r_a)
                V.scalar_tensor_tensor(out=row_out[:, 0:NE], in0=r_b, scalar=float(NT), in1=r_a,
                                       op0=ALU.mult, op1=ALU.add).then_inc(rows_r, 1)

            first_slots(0, link)
            link(V.tensor_reduce(m_1[:, 0, :], ps[:, PLACES, TILES * NE:(TILES + 1) * NE], AX.X, ALU.max))
            V.tensor_copy(most[:, :], m_1[:, 0, :]).then_inc(most_r, 1)
            dve.wait_ge(most_r, 1)
            dve.wait_ge(ge_s, 1)
            link(V.tensor_reduce(s_g, grp_w, AX.X, ALU.add))
            dve.wait_ge(e2_s, 1)
            link(V.tensor_scalar(m_1, e_2, 1.0, None, ALU.add))
            link(V.tensor_tensor(m_1, m_1, s_g, ALU.mult))
            link(V.reciprocal(cw[:, 0, :], m_1.rearrange("p t o -> p (t o)")))
            link(V.tensor_tensor(cw[:, 1, :], cw[:, 0, :], e_2.rearrange("p t o -> p (t o)"), ALU.mult))
            def low_x(x):
                dve.wait_ge(xhi_done, x + 1)
                src = p_x.rearrange("p b (k s) -> p (b k) s", s=P)
                for e in range(2):
                    cut = slice(e * SLOTS, (e + 1) * SLOTS)
                    V.tensor_tensor(xr[:, :, e, 1, 0:SLOTS], src[:, :, cut],
                                    xr[:, :, e, 0, 0:SLOTS].bitcast(F32), ALU.subtract)
                    last = V.tensor_copy(xz[:, :, e, 0:SLOTS], src[:, UBLOCKS - 1:KC:UBLOCKS, cut])
                last.then_inc(xr_ready, 1)

            def add_y(x):
                dve.wait_ge(y_copied, x + 1)
                need(dve, y_scat, x * 16)
                V.tensor_tensor(yo[:, :].rearrange("p (b n) -> p b n", b=2), p_y[0:SLOTS, :, :],
                                yc[:, :].rearrange("p (b n) -> p b n", b=2), ALU.add).then_inc(y_added, 1)

            steps = [link]

            def low_w(n, u, first, last):
                dve.wait_ge(hi_ready, n * UNITS + u + 1)
                wait_for_buffer(dve, n, u, last, LO_RING)
                off = (u % 2) * UBLOCKS * BLOCK
                V.tensor_tensor(lo[:, u % LO_RING, :], ring[:, u // 2, off:off + SPLIT],
                                hi[:, u % HI_RING, :].bitcast(F32),
                                ALU.subtract).then_inc(lo_ready, counted(u, first, last))

            def hidden(x, units):
                dve.wait_ge(silu_done, x + 1)
                need(dve, unit_done, units)
                V.tensor_tensor(h32[:, :, 0:SLOTS], sg[:, :, :], p_t[:, 1], ALU.mult).then_inc(h_step, 1)
                dve.wait_ge(h_step, x * 2 + 1)
                V.tensor_copy(hr[:, :, 0, 0:SLOTS], h32[:, :, 0:SLOTS]).then_inc(h_step, 1)
                dve.wait_ge(h_step, x * 2 + 2)
                V.tensor_tensor(hr[:, :, 1, 0:SLOTS], h32[:, :, 0:SLOTS],
                                hr[:, :, 0, 0:SLOTS].bitcast(F32), ALU.subtract).then_inc(hr_ready, 1)

            def step(n, i, q, first, last):
                x = (q * PAIRS + i) * 2

                def low(*units):
                    for u in units:
                        low_w(n, u, first, last)

                if isinstance(n, int) and n == 0:
                    dve.wait_ge(v_out, 16)
                    dve.wait_ge(wo_s, 3)
                    low(0, 1)
                    low_x(0)
                    choose(NE)
                    low(2)
                elif not last:
                    low_x(q * PAIRS + i)
                    low(0, 1)
                    if first:
                        choose(NE)
                    low(2)
                if last:
                    low(4)
                if not first:
                    add_y(x - 2)
                if not last:
                    low(3)
                if first:
                    all_slots(q, steps[0])
                if not first:
                    hidden(x - 1, n * UNITS)
                    low(*((5,) if last else (4, 5)))
                if not last:
                    low(6, 7, 8, 9)
                if not first:
                    add_y(x - 1)
                if not last:
                    low(10)
                    hidden(x, n * UNITS + 6)
                    low(11)

            def one_pass(q):
                if not isinstance(q, int):
                    count = [0]
                    each = 6

                    def step_q(ins):
                        count[0] += 1
                        ins.then_inc(pass_c, 1)
                        dve.wait_ge(pass_c, (q - 1) * each + count[0])
                    step_q(V.tensor_scalar(place[:, :, :], place[:, :, :], float(-SLOTS), None, ALU.add))
                    first_slots(q, step_q)
                    steps[0] = step_q
                over_rounds(dve, q, step)

            over_pass(dve, one_pass)
            V.memset(spare[:, 1:2], 0.0).then_inc(experts_done, 1)

            dve.wait_ge(gl_in, 32)
            for t, r in enumerate(ROWS):
                for c in range(2):
                    dve.wait_ge(moe_in[t][c], 16)
                    V.scalar_tensor_tensor(out=h[0:r, t, :], in0=ring[0:r, c, t * D:(t + 1) * D],
                                           scalar=cw[0:r, c, t:t + 1], in1=h[0:r, t, :], op0=ALU.mult,
                                           op1=ALU.add).then_inc(h2_s, 1)
                    dve.wait_ge(h2_s, 2 * t + c + 1)
                V.tensor_tensor(perm[0:r, t].rearrange("p k q -> p q k"),
                                h[0:r, t, :].rearrange("p (q k) -> p q k", k=KC),
                                ring[0:r, 5, 0:D].rearrange("p (q k) -> p q k", k=KC), ALU.mult).then_inc(nrm2, 1)
                mean_square(t, r, 0, sq2, ms2, 0)
                dve.wait_ge(rt2, t + 1)
                if t < TILES - 1:
                    V.reciprocal(stat[0:r, 3, t:t + 1], stat[0:r, 2, t:t + 1]).then_inc(scale2, 1)
                else:
                    link(V.reciprocal(stat[0:r, 3, t:t + 1], stat[0:r, 2, t:t + 1]))
                    V.tensor_copy(stat[NS:P, 3, t:t + 1], stat[0:NS, 3, t:t + 1]).then_inc(scale2, 1)
                dve.wait_ge(tr2, t + 1)
                V.tensor_copy(nT[:, :, t * P:t * P + r],
                              ps[:, 6:8, :].rearrange("p b (k s) -> p (b k) s", s=P)[:, :, 0:r]).then_inc(cp2, 1)
            for t, r in enumerate(ROWS):
                sig = (mixT[0:r, :, :].rearrange("p a b -> p (a b)") if t != 1 else win_flat[0:r, :])[:, 0:D]
                for half in range(2):
                    cut = slice(half * BLOCK, (half + 1) * BLOCK)
                    dve.wait_ge(sig_s, 2 * t + half + 1)
                    link(V.tensor_tensor(ple[0:r, t, cut], ple[0:r, t, cut], sig[:, cut], ALU.mult))
                    V.tensor_tensor(h[0:r, t, cut], h[0:r, t, cut], ple[0:r, t, cut], ALU.add).then_inc(h3_s, 1)
                norm_rows(t, r, 8, sq2, ms2, rt2, 3, ring[:, 5, D:2 * D], ple[0:r, t, :], y_s)


_INS = ['x_prompt', 'x_sample', 'state_pool', 'p_prompt', 'p_sample', 'g_mix', 'w_in', 'w_pool',
        'pool_scale', 'g_v', 'b_v', 'w_spatial', 'b_spatial', 'w_out', 'g_ffn', 'w_rg', 'b_rg', 'w_re',
        'b_re', 'w_eg', 'w_eu', 'w_ed', 'w_ple', 'g_ple', 'w_ple_gate', 'g_final']
_OUTS = [(1, SEQ, D), (DEC_B, DEC_L, D), (1, 1, HIST, W), (1, DEC_B, HIST, W), (1, DEC_B, DEC_L, W)]


def kernel(**inputs):
    import concourse.bacc as bacc
    from concourse.bass_utils import run_bass_kernel_spmd

    nc = bacc.Bacc("TRN2", target_bir_lowering=False, num_devices=1)
    arrays, args = {}, []
    for name in _INS:
        a = np.ascontiguousarray(inputs[name])
        arrays[f"in_{name}_dram"] = a
        args.append(nc.dram_tensor(f"in_{name}_dram", a.shape, mybir.dt.from_np(a.dtype),
                                   kind="ExternalInput").ap())
    for i, shape in enumerate(_OUTS):
        args.append(nc.dram_tensor(f"out_{i}_dram", shape, F32, kind="ExternalOutput").ap())
    build(nc, *args)
    r = run_bass_kernel_spmd(nc, [arrays], core_ids=[0])
    return tuple(r.results[0][f"out_{i}_dram"] for i in range(len(_OUTS)))
```
